# Optimizing a Trainium2 kernel written in Bass

```python
import math
import jax, jax.numpy as jnp
from jax import lax
import numpy as np

D_MODEL = 2048
BATCH = 1
SEQ = 256
DEPTH = 1

SB_HEADS = 8
SB_HEAD_DIM = 128
SB_WIDTH = SB_HEADS * SB_HEAD_DIM
MLA_HEADS = 8
MLA_NOPE_DIM = 128
MLA_ROPE_DIM = 64
MLA_V_DIM = 128
MLA_Q_RANK = 512
MLA_KV_RANK = 256
MLA_WIDTH = MLA_HEADS * MLA_V_DIM
MLA_QK_DIM = MLA_NOPE_DIM + MLA_ROPE_DIM
MIX_WIDTH = SB_WIDTH + MLA_WIDTH
ROPE_THETA = 10000.0
Q_BLOCK = 128
IN_PROJ_WIDTH = 3 * SB_WIDTH + MLA_Q_RANK + MLA_KV_RANK + MLA_ROPE_DIM
IN_SPLITS = [SB_WIDTH, 2 * SB_WIDTH, 3 * SB_WIDTH, 3 * SB_WIDTH + MLA_Q_RANK,
             3 * SB_WIDTH + MLA_Q_RANK + MLA_KV_RANK]
PEER_HEADS = 8
PEER_N_KEYS = 128
PEER_N_EXPERTS = PEER_N_KEYS * PEER_N_KEYS
PEER_QUERY_DIM = 256
PEER_HALF = PEER_QUERY_DIM // 2
PEER_TOPK = 16
PEER_CHUNK = 128
NORM_EPS = 1e-6

kernel_name = "hymba_sba_mla_peer_adaln_block"

def rmsnorm(x, g):
    xf = x.astype(jnp.float32)
    y = xf * lax.rsqrt(jnp.mean(xf * xf, axis=-1, keepdims=True) + NORM_EPS)
    return (y * g.astype(jnp.float32)).astype(x.dtype)

def rope_tables(positions, dtype):
    inv_freq = ROPE_THETA ** (-jnp.arange(0, MLA_ROPE_DIM, 2, dtype=jnp.float32) / MLA_ROPE_DIM)
    ang = positions.astype(jnp.float32)[..., None] * inv_freq
    return jnp.cos(ang).astype(dtype), jnp.sin(ang).astype(dtype)

def apply_rope(x, cos, sin):
    half = x.shape[-1] // 2
    x1, x2 = x[..., :half], x[..., half:]
    return jnp.concatenate([x1 * cos - x2 * sin, x2 * cos + x1 * sin], axis=-1)

def stick_breaking_attention(q, k, v):
    seq = q.shape[1]
    scale = SB_HEAD_DIM ** -0.5
    outs = []
    for blk in range(seq // Q_BLOCK):
        start = blk * Q_BLOCK
        end = start + Q_BLOCK
        z = jnp.einsum('bqhd,bkhd->bhqk', q[:, start:end], k[:, :end]).astype(jnp.float32) * scale
        t_idx = start + jnp.arange(Q_BLOCK)[:, None]
        s_idx = jnp.arange(end)[None, :]
        mask = s_idx < t_idx
        log_one_minus = jnp.where(mask, jax.nn.log_sigmoid(-z), 0.0)
        between = lax.cumsum(log_one_minus, axis=3, reverse=True) - log_one_minus
        weights = jnp.where(mask, jnp.exp(jax.nn.log_sigmoid(z) + between), 0.0)
        outs.append(jnp.einsum('bhqk,bkhd->bqhd', weights.astype(v.dtype), v[:, :end]))
    return jnp.concatenate(outs, axis=1)

def mla_attention(q_nope, q_pe, k_nope, k_pe, v):
    seq = q_nope.shape[1]
    scale = MLA_QK_DIM ** -0.5
    outs = []
    for blk in range(seq // Q_BLOCK):
        start = blk * Q_BLOCK
        end = start + Q_BLOCK
        s = (jnp.einsum('bqhd,bkhd->bhqk', q_nope[:, start:end], k_nope[:, :end])
             + jnp.einsum('bqhr,bkr->bhqk', q_pe[:, start:end], k_pe[:, :end]))
        s = s.astype(jnp.float32) * scale
        t_idx = start + jnp.arange(Q_BLOCK)[:, None]
        s_idx = jnp.arange(end)[None, :]
        s = jnp.where(s_idx <= t_idx, s, -jnp.inf)
        p = jax.nn.softmax(s, axis=-1)
        outs.append(jnp.einsum('bhqk,bkhd->bqhd', p.astype(v.dtype), v[:, :end]))
    return jnp.concatenate(outs, axis=1)

def peer_ffn(h, w_q, keys1, keys2, u_tab, v_tab):
    b, s, d = h.shape
    q = jnp.einsum('bsd,dq->bsq', h, w_q).reshape(b, s, PEER_HEADS, 2, PEER_HALF)
    s1 = jnp.einsum('bshq,hnq->bshn', q[..., 0, :], keys1)
    s2 = jnp.einsum('bshq,hnq->bshn', q[..., 1, :], keys2)
    v1, i1 = lax.top_k(s1, PEER_TOPK)
    v2, i2 = lax.top_k(s2, PEER_TOPK)
    cand = (v1[..., :, None] + v2[..., None, :]).reshape(b, s, PEER_HEADS, PEER_TOPK * PEER_TOPK)
    cand_idx = (i1[..., :, None] * PEER_N_KEYS + i2[..., None, :]).reshape(b, s, PEER_HEADS, PEER_TOPK * PEER_TOPK)
    best, pos = lax.top_k(cand, PEER_TOPK)
    expert_idx = jnp.take_along_axis(cand_idx, pos, axis=-1)
    gates = jax.nn.softmax(best.astype(jnp.float32), axis=-1).astype(h.dtype)
    n_blk = (b * s) // PEER_CHUNK
    hc = h.reshape(n_blk, PEER_CHUNK, d)
    ic = expert_idx.reshape(n_blk, PEER_CHUNK, PEER_HEADS, PEER_TOPK)
    gc = gates.reshape(n_blk, PEER_CHUNK, PEER_HEADS, PEER_TOPK)

    def block_fn(args):
        hx, ix, gx = args
        u = jnp.take(u_tab, ix, axis=0)
        act = jax.nn.gelu(jnp.einsum('chkd,cd->chk', u, hx), approximate=False)
        vv = jnp.take(v_tab, ix, axis=0)
        return jnp.einsum('chk,chkd->cd', gx * act, vv)

    y = lax.map(block_fn, (hc, ic, gc))
    return y.reshape(b, s, d)

def setup_inputs(seed: int = 0) -> dict:
    key = jax.random.key(seed)
    ks = jax.random.split(key, 24)
    f32 = jnp.float32
    D = D_MODEL

    def nrm(k, shape, scale):
        return jax.random.normal(k, shape, f32) * scale

    def gain(k, shape):
        return 1.0 + 0.02 * jax.random.normal(k, shape, f32)

    offset = jax.random.randint(ks[2], (BATCH, 1), 0, 1024, dtype=jnp.int32)
    positions = (offset + jnp.arange(SEQ, dtype=jnp.int32)[None, :]).astype(jnp.int32)
    return {
        "x": nrm(ks[0], (BATCH, SEQ, D), 1.0),
        "c": nrm(ks[1], (BATCH, D), 1.0),
        "positions": positions,
        "w_ada": nrm(ks[3], (DEPTH, D, 6 * D), D ** -0.5),
        "b_ada": nrm(ks[4], (DEPTH, 6 * D), 0.02),
        "norm1_g": gain(ks[5], (DEPTH, D)),
        "w_in": nrm(ks[6], (DEPTH, D, IN_PROJ_WIDTH), D ** -0.5),
        "mla_q_norm_g": gain(ks[7], (DEPTH, MLA_Q_RANK)),
        "w_uq": nrm(ks[8], (DEPTH, MLA_Q_RANK, MLA_HEADS * MLA_QK_DIM), MLA_Q_RANK ** -0.5),
        "mla_kv_norm_g": gain(ks[9], (DEPTH, MLA_KV_RANK)),
        "w_ukv": nrm(ks[10], (DEPTH, MLA_KV_RANK, MLA_HEADS * (MLA_NOPE_DIM + MLA_V_DIM)), MLA_KV_RANK ** -0.5),
        "out_norm_sba_g": gain(ks[11], (DEPTH, SB_WIDTH)),
        "out_norm_mla_g": gain(ks[12], (DEPTH, MLA_WIDTH)),
        "w_o": nrm(ks[13], (DEPTH, MIX_WIDTH, D), MIX_WIDTH ** -0.5),
        "norm2_g": gain(ks[14], (DEPTH, D)),
        "w_peer_q": nrm(ks[15], (DEPTH, D, PEER_HEADS * PEER_QUERY_DIM), D ** -0.5),
        "peer_keys1": nrm(ks[16], (DEPTH, PEER_HEADS, PEER_N_KEYS, PEER_HALF), PEER_HALF ** -0.5),
        "peer_keys2": nrm(ks[17], (DEPTH, PEER_HEADS, PEER_N_KEYS, PEER_HALF), PEER_HALF ** -0.5),
        "peer_u": nrm(ks[18], (DEPTH, PEER_N_EXPERTS, D), D ** -0.5),
        "peer_v": nrm(ks[19], (DEPTH, PEER_N_EXPERTS, D), PEER_HEADS ** -0.5),
        "final_norm_g": gain(ks[20], (D,)),
    }

def reference(x, c, positions, w_ada, b_ada, norm1_g, w_in, mla_q_norm_g, w_uq, mla_kv_norm_g, w_ukv,
              out_norm_sba_g, out_norm_mla_g, w_o, norm2_g, w_peer_q, peer_keys1, peer_keys2,
              peer_u, peer_v, final_norm_g):
    b, s, d = x.shape
    cos, sin = rope_tables(positions, x.dtype)
    c_act = jax.nn.silu(c)
    for l in range(DEPTH):
        mod = (c_act @ w_ada[l] + b_ada[l])[:, None, :]
        sh1, sc1, g1, sh2, sc2, g2 = jnp.split(mod, 6, axis=-1)

        h = rmsnorm(x, norm1_g[l]) * (1.0 + sc1) + sh1
        proj = h @ w_in[l]
        sq, sk, sv, cq, ckv, kr = jnp.split(proj, IN_SPLITS, axis=-1)

        sb_out = stick_breaking_attention(
            sq.reshape(b, s, SB_HEADS, SB_HEAD_DIM),
            sk.reshape(b, s, SB_HEADS, SB_HEAD_DIM),
            sv.reshape(b, s, SB_HEADS, SB_HEAD_DIM)).reshape(b, s, SB_WIDTH)

        q = (rmsnorm(cq, mla_q_norm_g[l]) @ w_uq[l]).reshape(b, s, MLA_HEADS, MLA_QK_DIM)
        q_nope = q[..., :MLA_NOPE_DIM]
        q_pe = apply_rope(q[..., MLA_NOPE_DIM:], cos[:, :, None, :], sin[:, :, None, :])
        kv = (rmsnorm(ckv, mla_kv_norm_g[l]) @ w_ukv[l]).reshape(b, s, MLA_HEADS, MLA_NOPE_DIM + MLA_V_DIM)
        k_nope = kv[..., :MLA_NOPE_DIM]
        v_mla = kv[..., MLA_NOPE_DIM:]
        k_pe = apply_rope(kr, cos, sin)
        mla_out = mla_attention(q_nope, q_pe, k_nope, k_pe, v_mla).reshape(b, s, MLA_WIDTH)

        mixed = jnp.concatenate([rmsnorm(sb_out, out_norm_sba_g[l]),
                                 rmsnorm(mla_out, out_norm_mla_g[l])], axis=-1) @ w_o[l]
        x = x + g1 * mixed

        h2 = rmsnorm(x, norm2_g[l]) * (1.0 + sc2) + sh2
        x = x + g2 * peer_ffn(h2, w_peer_q[l], peer_keys1[l], peer_keys2[l], peer_u[l], peer_v[l])
    return rmsnorm(x, final_norm_g)


_drawn_inputs = setup_inputs


def setup_inputs(seed=0):
    import zlib

    import numpy as np

    out = dict(_drawn_inputs(seed))
    spreads = {}
    factors = {'norm1_g': 3.943,
     'mla_q_norm_g': 8.0,
     'mla_kv_norm_g': 4.349,
     'out_norm_sba_g': 14.246,
     'out_norm_mla_g': 14.623,
     'norm2_g': 10.403,
     'final_norm_g': 8.47}
    for name, (base, spread) in spreads.items():
        noise = np.random.default_rng([zlib.crc32(name.encode()), seed]).standard_normal(out[name].shape)
        drawn = base * np.exp(spread * noise) if base else spread * noise
        out[name] = __import__('jax').numpy.asarray(drawn.astype(out[name].dtype))
    for name, factor in factors.items():
        out[name] = (out[name] * factor).astype(out[name].dtype)
    return out
```

```python
import math
from contextlib import ExitStack

import numpy as np

import concourse.bass as bass
from concourse import mybir

ALU = mybir.AluOpType
ACT = mybir.ActivationFunctionType
AX = mybir.AxisListType
F32 = mybir.dt.float32
F32R = mybir.dt.float32r
I32 = mybir.dt.int32
U32 = mybir.dt.uint32

P = 128
D = 2048
KC = D // P
T = 256
TT = T // P
H = 8
QR, KVR, ROPE, HALF = 512, 256, 64, 32
NK = 128
TOPK = 16
SB_SCALE = 128 ** -0.5
MLA_SCALE = 192 ** -0.5
EPS = 1e-6
NEG = -1e30
NTILES = NK
QP = P // 4
KB = 1024


def build(nc, x, c, positions, w_ada, b_ada, norm1_g, w_in, mla_q_norm_g, w_uq, mla_kv_norm_g,
          w_ukv, out_norm_sba_g, out_norm_mla_g, w_o, norm2_g, w_peer_q, peer_keys1, peer_keys2,
          peer_u, peer_v, final_norm_g, out):
    ctx = ExitStack()
    nc_sem = lambda name: ctx.enter_context(nc.semaphore(name))

    BASE = 16512
    A, B, C, E = BASE, BASE + 128 * KB, BASE + 172 * KB, BASE + 196 * KB

    def at(name, offset, shape, dtype=F32):
        return nc.alloc_sbuf_tensor_at(name, shape, dtype, offset=offset)

    e_next = [E]

    def small(name, shape, dtype=F32):
        size = 4 * int(np.prod(shape[1:]))
        t = at(name, e_next[0], shape, dtype)
        e_next[0] += (size + 31) // 32 * 32
        return t

    ring = [at(f"ring{s}", A + 32 * KB * s, [P, 32 * KB // 4]) for s in range(3)]
    xs = at("xs", A + 96 * KB, [P, TT, D])
    sbq = at("sbq", A + 96 * KB, [P, H, T])
    sbk = at("sbk", A + 104 * KB, [P, H, T])
    x2 = at("x2", A + 96 * KB, [P, TT, D])
    s_all = at("s_all", A + 96 * KB, [P, TT, 2 * H, NK])
    hT = at("hT", A + 112 * KB, [P, KC, T])
    mix = at("mix", A + 112 * KB, [P, 2 * H, T])
    h2T = at("h2T", A + 112 * KB, [P, KC, T])
    qnT = at("qnT", B, [P, H, T])
    knT = at("knT", B + 8 * KB, [P, H, T])
    vm = at("vm", B + 16 * KB, [P, TT, H * P])
    sbv = at("sbv", B + 24 * KB, [P, TT, H * P])
    qpeT = at("qpeT", B + 32 * KB, [P, H // 2, T])
    kpeT = at("kpeT", B + 36 * KB, [P, 2, T])
    tri = at("tri", B + 38 * KB, [P, P])
    mask_sb = at("mask_sb", B + 38 * KB + 512, [P, P])
    mask_mla = at("mask_mla", B + 39 * KB, [P, 3 * P])
    trig = at("trig", B + 40 * KB + 512, [P, 8, TT * HALF])
    lat = at("lat", C, [P, TT, QR + KVR + ROPE])
    cqT = at("cqT", C + 7 * KB, [P, QR // P, T])
    ckvT = at("ckvT", C + 11 * KB, [P, KVR // P, T])
    qpe = at("qpe", C + 13 * KB, [P, TT, H * ROPE])
    kpad = at("kpad", C + 17 * KB, [P, 2, TT, P])
    vrow = at("vrow", C, [P, 2, P])
    junk = at("junk", B, [P, D])
    acc = at("acc", C + 20 * KB, [P, 2, 512])
    za = [at(f"za{k}", C + 4608 * k, [P, 3, 384]) for k in range(2)]
    ma = [at(f"ma{k}", C + 9216 + 3072 * k, [P, 2, 384]) for k in range(2)]
    sq = at("sq", C + 9216 + 6144, [P, 2, T])
    xs2 = at("xs2", C, [P, TT, D])
    g1b = at("g1b", C + 16 * KB, [P, D])
    knat = at("knat", B, [P, 2, H, P])
    rs_g = at("rs_g", B + 32 * KB, [P, 2, T])
    tmpo = at("tmpo", B + 34 * KB, [P, 2, 512])
    junk2 = at("junk2", B + 38 * KB, [P, 512])
    acc4 = at("acc4", B + 40 * KB, [P, 2, 512])
    h2s = at("h2s", B, [P, KC, 2, T], F32R)
    kT = at("kT", B + 32 * KB, [P, 2 * H, P])
    pq = at("pq", B + 40 * KB, [P, 2, 2, T])
    hid = at("hid", A, [P, NTILES, T])
    uT = [at(f"uT{g}", B + 32 * KB + 2 * KB * g, [P, 512]) for g in range(4)]
    ulo = [at(f"ulo{g}", B + 32 * KB + 2 * KB * g, [P, 512], F32R) for g in range(4)]
    ubuf = [at(f"ubuf{s}", C + 8 * KB * s, [P, D]) for s in range(3)]
    wk = at("wk", A + 112 * KB, [P, 2, 2, NK])
    cand = at("cand", A + 114 * KB, [P, 2, TOPK * TOPK])
    oh = at("oh", A + 116 * KB, [P, 2 * TOPK, TOPK])
    tk_v = at("tk_v", A + 118 * KB, [P, 3, TOPK])
    tk_i = at("tk_i", A + 118 * KB + 192, [P, 3, TOPK], U32)
    tk_ab = at("tk_ab", A + 118 * KB + 384, [P, 2, TOPK], U32)
    tk_f = at("tk_f", A + 118 * KB + 512, [P, 4, TOPK])
    best = at("best", A + 119 * KB, [P, TT * H, TOPK])
    selT = at("selT", B + 32 * KB, [P, 3, T])
    oneh1 = at("oneh1", B, [P, 2, 4, NK])
    oneh2 = at("oneh2", B + 4 * KB, [P, 2, 4, NK])
    negT = at("negT", B + 8 * KB, [P, T])
    slot = at("slot", B + 9 * KB, [P, 2, 3])
    vhi = at("vhi", B, [P, 2, D], F32R)
    vlo = at("vlo", B + 16 * KB, [P, 2, D], F32R)
    asp = at("asp", B + 36 * KB, [P, 3, 2, T], F32R)
    g2row = at("g2row", A + 124 * KB, [KC, P])
    x2r = at("x2r", A, [P, TT, D])
    g2b = at("g2b", A + 16 * KB, [P, D])
    fgb = at("fgb", A + 24 * KB, [P, D])
    yo = at("yo", A + 32 * KB, [P, TT, D])
    junk3 = at("junk3", A + 48 * KB, [P, 2, 512])

    ident = small("ident", [P, P])
    ones = small("ones", [P, P])
    iota = small("iota", [P, P])
    iota16 = small("iota16", [P, TOPK])
    vcA = small("vcA", [P, P])
    vcB = small("vcB", [P, 38])
    modc = small("modc", [P, 96])
    cact = small("cact", [P, KC])
    a1c = small("a1c", [P, KC])
    a2q = small("a2q", [P, KC])
    sh2q = small("sh2q", [P, KC])
    posi = small("posi", [P, TT], I32)
    st = small("st", [P, 16])
    mxd = small("mxd", [P, 2, 8])
    sel = small("sel", [P, 2, TT * H, TOPK])
    gate = small("gate", [P, TT * H, TOPK])
    e_next[0] = (e_next[0] + 31) // 32 * 32
    rt = at("rt", e_next[0], [P, 2, H * HALF])
    uhi = [at(f"uhi{g}", B + 40 * KB + 2 * KB * g, [P, 512], F32R) for g in range(2)]
    uhi += [small(f"uhi{g}", [P, 512], F32R) for g in (2, 3)]
    gsum = small("gsum", [P, 2, TT * H])
    assert e_next[0] <= 229368, e_next[0]

    ps = nc.alloc_psum_tensor("ps", [P, 8, 512], F32)
    x2_dram = nc.dram_tensor("x2_scratch", (P, TT * D), F32, kind="Internal").ap()
    g2_dram = nc.dram_tensor("g2_scratch", (1, D), F32, kind="Internal").ap()

    filled = [nc_sem(f"bank{b}_filled") for b in range(8)]
    emptied = [nc_sem(f"bank{b}_emptied") for b in range(8)]
    unit, used = {}, [0] * 8

    def plan(names, banks):
        for k, name in enumerate(names):
            b = banks[k % len(banks)]
            unit[name] = (b, used[b])
            used[b] += 1

    def take(pe, name):
        b, o = unit[name]
        if o:
            pe.wait_ge(emptied[b], o)
        return ps[:, b, :]

    def fill(ins, name):
        ins.then_inc(filled[unit[name][0]], 1)

    def full(eng, name):
        b, o = unit[name]
        eng.wait_ge(filled[b], o + 1)
        return ps[:, b, :]

    def empty(ins, name):
        ins.then_inc(emptied[unit[name][0]], 1)

    def copied(eng, name):
        b, o = unit[name]
        eng.wait_ge(emptied[b], o + 1)

    class Steps:

        def __init__(self, name):
            self.sem, self.n = nc_sem(name), 0

        def add(self, ins):
            ins.then_inc(self.sem, 1)
            self.n += 1
            return self.n

        def wait(self, eng, n=None):
            eng.wait_ge(self.sem, self.n if n is None else n)

    vec_steps, act_steps, pool_steps = Steps("vector_steps"), Steps("scalar_steps"), Steps("gpsimd_steps")

    ada_view = w_ada[0].rearrange("(kc p) n -> p kc n", p=P)
    ring_loaded = [nc_sem(f"ring{s}_loaded") for s in range(3)]
    ring_loads = [[], [], []]
    ring_read = [[], [], []]
    item = {}
    ada_summed = nc_sem("ada_summed")
    ada_columns = nc_sem("ada_columns")

    def plan_load(name, slot, read_by, pieces=1):
        item[name] = (slot, len(ring_loads[slot]))
        ring_loads[slot].append((ring_loads[slot] or [0])[-1] + pieces)
        ring_read[slot].append(read_by)

    def load(eng, name, *pieces):
        slot, n = item[name]
        if n:
            eng.wait_ge(*ring_read[slot][n - 1])
        for dst, src in pieces:
            eng.dma_start(dst, src).then_inc(ring_loaded[slot], 16)

    def loaded(eng, name):
        slot, n = item[name]
        eng.wait_ge(ring_loaded[slot], 16 * ring_loads[slot][n])
        return ring[slot]

    def unit_read(name):
        return (filled[unit[name][0]], unit[name][1] + 1)

    KH = KC // 2
    HALVED = 8
    ada_part_loaded = [nc_sem(f"ada_part{a}_loaded") for a in range(2)]
    ada_half_summed = nc_sem("ada_half_summed")

    def ada_load(eng, k):
        slot = item[f"ada{k}"][0]
        load(eng, f"ada{k}", (ring[slot][:, :].rearrange("p (kc n) -> p kc n", kc=KC),
                              ada_view[:, :, 512 * k:512 * k + 512]))

    def ada_load_parts(eng, k, first=False):
        for a in range(2):
            if not first:
                eng.wait_ge(*((ada_half_summed, k - HALVED), (ada_summed, k))[a])
            eng.dma_start(ring[2][:, 4096 * a:4096 * a + 4096].rearrange("p (kc n) -> p kc n", kc=KH),
                          ada_view[:, KH * a:KH * a + KH, 512 * k:512 * k + 512]).then_inc(ada_part_loaded[a], 16)

    def ada_sum(k, acc=acc):
        dve = nc.vector
        a = acc[:, k % 2, :]
        if k < HALVED:
            w = loaded(dve, f"ada{k}")[:, :].rearrange("p (kc n) -> p kc n", kc=KC)
        else:
            w = ring[2][:, :].rearrange("p (kc n) -> p kc n", kc=KC)
        if k >= 2:
            dve.wait_ge(ada_columns, k - 1)
        for kc in range(KC):
            if k >= HALVED and kc % KH == 0:
                dve.wait_ge(ada_part_loaded[kc // KH], 16 * (k - HALVED + 1))
            if kc == 0:
                ins = nc.vector.tensor_scalar(a, w[:, 0, :], cact[:, 0:1], None, ALU.mult)
            else:
                ins = nc.vector.scalar_tensor_tensor(out=a, in0=w[:, kc, :], scalar=cact[:, kc:kc + 1],
                                                     in1=a, op0=ALU.mult, op1=ALU.add)
            if k >= HALVED and kc == KH - 1:
                ins.then_inc(ada_half_summed, 1)
                dve.wait_ge(ada_half_summed, k - HALVED + 1)
            elif kc < KC - 1:
                vec_steps.add(ins)
                vec_steps.wait(dve)
        ins.then_inc(ada_summed, 1)

    def ada_cols(k, acc=acc):
        pe = nc.tensor
        pe.wait_ge(ada_summed, k + 1)
        for b in range(4):
            ins = nc.tensor.matmul(ps[:, 7, 4 * k + b:4 * k + b + 1], acc[:, k % 2, P * b:P * b + P],
                                   ones[:, 0:1], start=True, stop=True)
        ins.then_inc(ada_columns, 1)

    ada_bias = nc_sem("ada_bias_added")

    def ada_finish(part, count):
        nc.vector.wait_ge(ada_columns, 4 * (part + count))
        lo, hi = KC * part, KC * (part + count)
        nc.vector.tensor_tensor(modc[:, lo:hi], ps[:, 7, lo:hi], vcA[:, 32 + lo:32 + hi],
                                ALU.add).then_inc(ada_bias, 1)

    SH1, SC1, G1, SH2, SC2, G2 = (KC * k for k in range(6))

    n_in = H * P
    IN_ITEMS = [("cq", 3 * n_in, 512), ("ckv", 3 * n_in + QR, KVR + ROPE),
                ("q0", 0, 512), ("q1", 512, 512), ("k0", n_in, 512), ("k1", n_in + 512, 512),
                ("v0", 2 * n_in, 512), ("v1", 2 * n_in + 512, 512)]
    win_view = w_in[0].rearrange("(kc p) n -> p kc n", p=P)
    def load_group(eng, name, view, col, width, kc):
        slot = item[name][0]
        load(eng, name, (ring[slot][:, 0:kc * width].rearrange("p (kc n) -> p kc n", kc=kc),
                         view[:, :, col:col + width]))

    const_ready, vec_loaded, x_loaded, pos_loaded = map(nc_sem, ("const_ready", "vec_loaded", "x_loaded", "pos_loaded"))
    silu_exp, silu_ready, mod1_ready, row_var, row_std, row_rstd = map(
        nc_sem, ("silu_exp", "silu_ready", "mod1_ready", "row_var", "row_std", "row_rstd"))
    for k in range(8):
        plan_load(f"ada{k}", 1 + k % 2, (ada_summed, k + 1))
    plan(["vecA", "vecB"], [0, 1])
    names = [f"hT{u}" for u in range(8)]
    for name, _, _ in IN_ITEMS:
        names += [f"{name}_{i}" for i in range(2)]
    names += ["cqT0", "cqT1", "ckvT", "kpeT"] + [f"uq{u}" for u in range(4)] + ["qpe0", "qpe1"]
    names += [f"kn{u}" for u in range(4)] + [f"vm{u}" for u in range(4)] + ["qpeT0", "qpeT1"]
    plan(names, [2, 3, 4, 5, 6, 0, 1])
    for k, (name, _, _) in enumerate(IN_ITEMS):
        plan_load(name, k % 2, unit_read(f"{name}_1"))
    plan_load("w_uq", 0, unit_read("qpe1"))
    plan_load("w_ukv", 1, unit_read("vm3"))
    attention_order = []
    for k in range(2 * H + 4):
        attention_order += [f"{kind}{k - lag}" for kind, lag in (("z", 0), ("r", 2), ("o", 4)) if 0 <= k - lag < 2 * H]
    plan(attention_order, [0, 1, 2, 3, 4])
    plan([f"gb{g}" for g in range(4)] + [f"w{n}_{t}" for n in range(4) for t in range(TT)]
         + [f"h2T{u}" for u in range(8)] + [f"kT{u}" for u in range(4)] + ["p0"]
         + [f"{w}{u + (w == 'p')}" for u in range(7) for w in ("p", "sc")] + ["sc7", "g2r"], [0, 1, 2, 3, 4])
    for n in range(4):
        plan_load(f"w_o{n}", n % 2, unit_read(f"w{n}_1"))
    for n in range(4):
        plan_load(f"w_pq{n}", n % 2, unit_read(f"p{2 * n + 1}"), pieces=4)
    x_view = x[0].rearrange("(t p) d -> p t d", p=P)
    VA = [(norm1_g, 0, 16), (norm2_g, 16, 16), (b_ada, 32, 96)]
    VB = [(c, 0, 16), (mla_q_norm_g, 16, 4), (mla_kv_norm_g, 20, 2), (out_norm_sba_g, 22, 8), (out_norm_mla_g, 30, 8)]
    inv_freq = (np.float32(10000.0) ** (-np.arange(0, ROPE, 2, dtype=np.float32) / np.float32(ROPE))).astype(np.float32)

    with nc.Block() as block:
        @block.sync
        def _(sp):
            for k, vecs in enumerate((VA, VB)):
                for v, r, n in vecs:
                    sp.dma_start(vrow[r:r + n, k, :], v[0].rearrange("(r q) -> r q", q=P)).then_inc(vec_loaded, 16)
            sp.dma_start(xs[:, :, :], x_view).then_inc(x_loaded, 16)
            for k in range(8):
                ada_load(sp, k)
            name, col, width = IN_ITEMS[0]
            load_group(sp, name, win_view, col, width, KC)

        @block.gpsimd
        def _(pool):
            with nc.allow_non_contiguous_dma(reason="256 positions"):
                pool.dma_start(posi[:, :], positions[0].rearrange("(t p) -> p t", p=P)).then_inc(pos_loaded, 16)
            st_ = pool_steps
            st_.add(nc.gpsimd.memset(ident[:, :], 0.0))
            st_.add(nc.gpsimd.memset(ones[:, :], 1.0))
            st_.add(nc.gpsimd.memset(tri[:, :], 1.0))
            st_.add(nc.gpsimd.memset(mask_sb[:, :], 1.0))
            st_.add(nc.gpsimd.memset(mask_mla[:, :], 0.0))
            st_.wait(pool)
            st_.add(nc.gpsimd.affine_select(out=ident[:, :], in_=ident[:, :], compare_op=ALU.not_equal, fill=1.0,
                                            base=0, pattern=[[-1, P]], channel_multiplier=1))
            st_.add(nc.gpsimd.affine_select(out=tri[:, :], in_=tri[:, :], compare_op=ALU.is_ge, fill=0.0,
                                            base=0, pattern=[[-1, P]], channel_multiplier=1))
            st_.add(nc.gpsimd.affine_select(out=mask_sb[:, :], in_=mask_sb[:, :], compare_op=ALU.is_gt, fill=0.0,
                                            base=0, pattern=[[1, P]], channel_multiplier=-1))
            for b in (0, 2):
                m = mask_mla[:, P * b:P * b + P]
                st_.add(nc.gpsimd.affine_select(out=m, in_=m, compare_op=ALU.is_ge, fill=NEG,
                                                base=0, pattern=[[-1, P]], channel_multiplier=1))
            for q in range(HALF):
                v = float(inv_freq[q])
                st_.add(nc.gpsimd.memset(trig[:, 0, q:q + 1], v))
            st_.add(nc.gpsimd.iota(iota[:, :], [[1, P]], base=0, channel_multiplier=0,
                                   allow_small_or_imprecise_dtypes=True))
            st_.add(nc.gpsimd.iota(iota16[:, :], [[1, TOPK]], base=0, channel_multiplier=0,
                                   allow_small_or_imprecise_dtypes=True))
            st_.wait(pool)
            nc.gpsimd.memset(kpad[:, :, :, :], 0.0).then_inc(const_ready, 1)

        @block.tensor
        def _(pe):
            pe.wait_ge(const_ready, 1)
            pe.wait_ge(vec_loaded, 16 * (len(VA) + len(VB)))
            fill(nc.tensor.transpose(take(pe, "vecA")[:, 0:P], vrow[:, 0, :], ident[:, :]), "vecA")
            fill(nc.tensor.transpose(take(pe, "vecB")[:, 0:38], vrow[0:38, 1, :], ident[0:38, 0:38]), "vecB")
            for k in range(8):
                ada_cols(k)

        @block.scalar
        def _(act):
            copied(act, "vecB")
            nc.scalar.activation(cact[:, :], vcB[:, 0:KC], ACT.Exp, scale=-1.0).then_inc(silu_exp, 1)
            act.wait_ge(x_loaded, 16)
            for t in range(TT):
                ins = nc.scalar.activation(junk[:, :], xs[:, t, :], ACT.Square, accum_out=st[:, t:t + 1])
                if t == 0:
                    act_steps.add(ins)
                    act_steps.wait(act)
            ins.then_inc(row_var, 1)
            act.wait_ge(row_var, 2)
            nc.scalar.activation(st[:, 2:4], st[:, 2:4], ACT.Sqrt).then_inc(row_std, 1)
            act.wait_ge(row_rstd, 1)
            for t in range(TT):
                act_steps.add(nc.scalar.activation(xs[:, t, :], xs[:, t, :], ACT.Copy, scale=st[:, 2 + t:3 + t]))

        @block.vector
        def _(dve):
            full(dve, "vecA")
            empty(nc.vector.tensor_copy(vcA[:, :], ps[:, unit["vecA"][0], 0:P]), "vecA")
            full(dve, "vecB")
            empty(nc.vector.tensor_copy(vcB[:, :], ps[:, unit["vecB"][0], 0:38]), "vecB")
            dve.wait_ge(silu_exp, 1)
            vec_steps.add(nc.vector.tensor_scalar_add(cact[:, :], cact[:, :], 1.0))
            vec_steps.wait(dve)
            vec_steps.add(nc.vector.reciprocal(cact[:, :], cact[:, :]))
            vec_steps.wait(dve)
            vec_steps.add(nc.vector.tensor_tensor(cact[:, :], cact[:, :], vcB[:, 0:KC], ALU.mult))
            vec_steps.wait(dve)
            for k in range(8):
                ada_sum(k)
                if k == 2:
                    dve.wait_ge(row_var, 1)
                    nc.vector.tensor_scalar(st[:, 2:4], st[:, 0:2], 1.0 / D, EPS, ALU.mult, ALU.add).then_inc(row_var, 1)
                    dve.wait_ge(row_std, 1)
                    nc.vector.reciprocal(st[:, 2:4], st[:, 2:4]).then_inc(row_rstd, 1)
            ada_finish(0, 2)
            dve.wait_ge(ada_bias, 1)
            nc.vector.scalar_tensor_tensor(out=a1c[:, :], in0=modc[:, SC1:SC1 + KC], scalar=1.0,
                                           in1=vcA[:, 0:KC], op0=ALU.add, op1=ALU.mult).then_inc(mod1_ready, 1)

    lat_ms, lat_var, lat_std, lat_rstd, lat_normed, kpad_ready, trig_arg, trig_ready, qpe_ready = map(
        nc_sem, ("lat_ms", "lat_var", "lat_std", "lat_rstd", "lat_normed", "kpad_ready", "trig_arg", "trig_ready", "qpe_ready"))
    wuq_view = w_uq[0].rearrange("(kc p) n -> p kc n", p=P)
    wukv_view = w_ukv[0].rearrange("(kc p) n -> p kc n", p=P)
    wo_view = w_o[0].rearrange("(kc p) n -> p kc n", p=P)
    wpq_view = w_peer_q[0].rearrange("(a b i) n -> a i b n", a=4, i=QP)

    def load_wpq(eng, n):
        w = ring[item[f"w_pq{n}"][0]][:, :].rearrange("p (b n) -> p b n", b=KC)
        load(eng, f"w_pq{n}", *((w[QP * a:QP * a + QP], wpq_view[a, :, :, 512 * n:512 * n + 512]) for a in range(4)))

    def group(eng, name, width, kc):
        return loaded(eng, name)[:, 0:kc * width].rearrange("p (kc n) -> p kc n", kc=kc)

    def contract(pe, name, half, lhs, rhs, kc):
        for k in range(kc):
            ins = nc.tensor.matmul(half, lhs(k), rhs(k), start=(k == 0), stop=(k == kc - 1))
        return ins

    with nc.Block() as block:
        @block.sync
        def _(sp):
            for name, col, width in IN_ITEMS[1:]:
                load_group(sp, name, win_view, col, width, KC)
            load_group(sp, "w_uq", wuq_view, 0, H * 192, QR // P)
            load_group(sp, "w_ukv", wukv_view, 0, 2 * n_in, KVR // P)

        @block.gpsimd
        def _(pool):
            for k in range(8, 16):
                ada_load_parts(pool, k, first=(k == 8))

        @block.tensor
        def _(pe):
            for u in range(8):
                bank = take(pe, f"hT{u}")
                for k in range(2):
                    for t in range(TT):
                        ins = nc.tensor.transpose(bank[:, T * k + P * t:T * k + P * t + P],
                                                  xs[:, t, P * (2 * u + k):P * (2 * u + k) + P], ident[:, :])
                fill(ins, f"hT{u}")
            for u in range(8):
                copied(pe, f"hT{u}")
            ada_next = [8]
            for name, _, width in IN_ITEMS:
                w = group(pe, name, width, KC)
                for i in range(2):
                    bank = take(pe, f"{name}_{i}")
                    if name[0] in "cv":
                        ins = contract(pe, name, bank[:, 0:width], lambda k: hT[:, k, P * i:P * i + P],
                                       lambda k: w[:, k, :], KC)
                    else:
                        for b in range(2):
                            ins = contract(pe, name, bank[:, T * b:T * b + T],
                                           lambda k: w[:, k, P * (2 * i + b):P * (2 * i + b) + P],
                                           lambda k: hT[:, k, :], KC)
                    fill(ins, f"{name}_{i}")
                if name != "cq":
                    ada_cols(ada_next[0])
                    ada_next[0] += 1
            ada_cols(15)
            pe.wait_ge(lat_normed, TT)
            for u in range(2):
                bank = take(pe, f"cqT{u}")
                for k in range(2):
                    for t in range(TT):
                        ins = nc.tensor.transpose(bank[:, T * k + P * t:T * k + P * t + P],
                                                  lat[:, t, P * (2 * u + k):P * (2 * u + k) + P], ident[:, :])
                fill(ins, f"cqT{u}")
            bank = take(pe, "ckvT")
            for k in range(2):
                for t in range(TT):
                    ins = nc.tensor.transpose(bank[:, T * k + P * t:T * k + P * t + P],
                                              lat[:, t, QR + P * k:QR + P * k + P], ident[:, :])
            fill(ins, "ckvT")
            pe.wait_ge(kpad_ready, 1)
            bank = take(pe, "kpeT")
            for k in range(2):
                for t in range(TT):
                    ins = nc.tensor.transpose(bank[:, T * k + P * t:T * k + P * t + P], kpad[:, k, t, :], ident[:, :])
            fill(ins, "kpeT")
            w = group(pe, "w_uq", H * 192, QR // P)
            copied(pe, "cqT0")
            copied(pe, "cqT1")
            for u in range(4):
                bank = take(pe, f"uq{u}")
                for b in range(2):
                    h = 2 * u + b
                    ins = contract(pe, "", bank[:, T * b:T * b + T], lambda k: w[:, k, 192 * h:192 * h + P],
                                   lambda k: cqT[:, k, :], QR // P)
                fill(ins, f"uq{u}")
            wr = w.rearrange("p kc (h n) -> p kc h n", h=H)
            for t in range(TT):
                bank = take(pe, f"qpe{t}")
                fill(contract(pe, "", bank[:, 0:512].rearrange("p (h n) -> p h n", h=H),
                              lambda k: cqT[:, k, P * t:P * t + P], lambda k: wr[:, k, :, P:192], QR // P), f"qpe{t}")
            w = group(pe, "w_ukv", 2 * n_in, KVR // P)
            copied(pe, "ckvT")
            for u in range(4):
                bank = take(pe, f"kn{u}")
                for b in range(2):
                    h = 2 * u + b
                    ins = contract(pe, "", bank[:, T * b:T * b + T], lambda k: w[:, k, 256 * h:256 * h + P],
                                   lambda k: ckvT[:, k, :], KVR // P)
                fill(ins, f"kn{u}")
            wr = w.rearrange("p kc (h n) -> p kc h n", h=H)
            for u in range(4):
                t, g = u // 2, u % 2
                bank = take(pe, f"vm{u}")
                fill(contract(pe, "", bank[:, 0:512].rearrange("p (h n) -> p h n", h=4),
                              lambda k: ckvT[:, k, P * t:P * t + P],
                              lambda k: wr[:, k, 4 * g:4 * g + 4, P:256], KVR // P), f"vm{u}")
            pe.wait_ge(qpe_ready, 2)
            for u in range(2):
                bank = take(pe, f"qpeT{u}")
                for k in range(2):
                    for t in range(TT):
                        ins = nc.tensor.transpose(bank[:, T * k + P * t:T * k + P * t + P],
                                                  qpe[:, t, P * (2 * u + k):P * (2 * u + k) + P], ident[:, :])
                fill(ins, f"qpeT{u}")

        @block.scalar
        def _(act):
            for u in range(0, 8, 2):
                bank = full(act, f"hT{u}")
                for k in range(2):
                    ch = 2 * u + k
                    ins = nc.scalar.activation(hT[:, ch, :], bank[:, T * k:T * k + T], ACT.Identity,
                                               bias=modc[:, SH1 + ch:SH1 + ch + 1], scale=a1c[:, ch:ch + 1])
                empty(ins, f"hT{u}")
            for t in range(TT):
                empty(nc.scalar.copy(lat[:, t, 0:QR], full(act, f"cq_{t}")[:, 0:QR]), f"cq_{t}")
            for t in range(TT):
                empty(nc.scalar.copy(lat[:, t, QR:], full(act, f"ckv_{t}")[:, 0:KVR + ROPE]), f"ckv_{t}")
            for t in range(TT):
                copied(act, f"cq_{t}")
                copied(act, f"ckv_{t}")
            for t in range(TT):
                for g, (lo, n) in enumerate(((0, QR), (QR, KVR))):
                    if t + g:
                        act_steps.wait(act)
                    ins = nc.scalar.activation(junk[:, 0:n], lat[:, t, lo:lo + n], ACT.Square,
                                               accum_out=st[:, 4 + 2 * t + g:5 + 2 * t + g])
                    if t + g < 2:
                        act_steps.add(ins)
            ins.then_inc(lat_ms, 1)
            act.wait_ge(trig_arg, 1)
            nc.scalar.activation(trig[:, 5:7, :], trig[:, 2:4, :], ACT.Sin).then_inc(trig_ready, 1)
            act.wait_ge(lat_var, 1)
            nc.scalar.activation(st[:, 4:8], st[:, 4:8], ACT.Sqrt).then_inc(lat_std, 1)
            act.wait_ge(lat_rstd, 1)
            for t in range(TT):
                act_steps.add(nc.scalar.activation(lat[:, t, 0:QR], lat[:, t, 0:QR], ACT.Copy, scale=st[:, 4 + 2 * t:5 + 2 * t]))
                nc.scalar.activation(lat[:, t, QR:QR + KVR], lat[:, t, QR:QR + KVR], ACT.Copy,
                                     scale=st[:, 5 + 2 * t:6 + 2 * t]).then_inc(lat_normed, 1)
            for dst, tag in ((sbq, "q"), (sbk, "k")):
                for g in range(2):
                    for i in range(2):
                        name = f"{tag}{g}_{i}"
                        h = 4 * g + 2 * i
                        empty(nc.scalar.copy(dst[:, h:h + 2, :].rearrange("p h t -> p (h t)"), full(act, name)), name)
            for g in range(2):
                for t in range(TT):
                    name = f"v{g}_{t}"
                    empty(nc.scalar.copy(sbv[:, t, 512 * g:512 * g + 512], full(act, name)), name)
            for name, dst, gcol in [("cqT0", cqT[:, 0:2, :], 16), ("cqT1", cqT[:, 2:4, :], 18), ("ckvT", ckvT[:, :, :], 20)]:
                bank = full(act, name)
                for k in range(2):
                    ins = nc.scalar.activation(dst[:, k, :], bank[:, T * k:T * k + T], ACT.Copy,
                                               scale=vcB[:, gcol + k:gcol + k + 1])
                empty(ins, name)
            empty(nc.scalar.copy(kpeT[:, :, :].rearrange("p h t -> p (h t)"), full(act, "kpeT")), "kpeT")
            for u in range(4):
                empty(nc.scalar.copy(qnT[:, 2 * u:2 * u + 2, :].rearrange("p h t -> p (h t)"), full(act, f"uq{u}")), f"uq{u}")
            for u in range(4):
                empty(nc.scalar.copy(knT[:, 2 * u:2 * u + 2, :].rearrange("p h t -> p (h t)"), full(act, f"kn{u}")), f"kn{u}")
            for u in range(4):
                t, g = u // 2, u % 2
                empty(nc.scalar.copy(vm[:, t, 512 * g:512 * g + 512], full(act, f"vm{u}")), f"vm{u}")
            for u in range(2):
                empty(nc.scalar.copy(qpeT[:, 2 * u:2 * u + 2, :].rearrange("p h t -> p (h t)"), full(act, f"qpeT{u}")), f"qpeT{u}")

        @block.vector
        def _(dve):
            v = vec_steps

            def step(ins):
                v.add(ins)
                v.wait(dve)

            for u in range(1, 8, 2):
                bank = full(dve, f"hT{u}")
                for k in range(2):
                    ch = 2 * u + k
                    ins = nc.vector.tensor_scalar(hT[:, ch, :], bank[:, T * k:T * k + T], a1c[:, ch:ch + 1],
                                                  modc[:, SH1 + ch:SH1 + ch + 1], ALU.mult, ALU.add)
                empty(ins, f"hT{u}")
            dve.wait_ge(pos_loaded, 16)
            step(nc.vector.tensor_copy(st[:, 8:10], posi[:, :]))
            for t in range(TT):
                v.add(nc.vector.tensor_scalar(trig[:, 1, HALF * t:HALF * t + HALF], trig[:, 0, 0:HALF],
                                              st[:, 8 + t:9 + t], None, ALU.mult))
            v.wait(dve)
            MAGIC = 1.5 * 2 ** 23
            C1, C2 = 6.28125, 0.0019350051879882812
            C3 = float(2 * math.pi - C1 - C2)
            for r, turn, shift in ((2, 0.0, 0.0), (3, 0.25, math.pi / 2)):
                step(nc.vector.tensor_scalar(trig[:, 4, :], trig[:, 1, :], 1 / (2 * math.pi), turn, ALU.mult, ALU.add))
                step(nc.vector.tensor_scalar(trig[:, 4, :], trig[:, 4, :], MAGIC, None, ALU.add))
                step(nc.vector.tensor_scalar(trig[:, 4, :], trig[:, 4, :], MAGIC, None, ALU.subtract))
                src = trig[:, 1, :]
                for part in (C1, C2, C3):
                    step(nc.vector.scalar_tensor_tensor(out=trig[:, r, :], in0=trig[:, 4, :], scalar=-part,
                                                        in1=src, op0=ALU.mult, op1=ALU.add))
                    src = trig[:, r, :]
                step(nc.vector.tensor_scalar(trig[:, r, :], trig[:, r, :], shift, 3.1415925, ALU.add, ALU.min))
                ins = nc.vector.tensor_scalar(trig[:, r, :], trig[:, r, :], -3.1415925, None, ALU.max)
                if r == 2:
                    step(ins)
            ins.then_inc(trig_arg, 1)
            sin, cos = trig[:, 5, :], trig[:, 6, :]

            ada_sum(8)
            ada_sum(9)
            dve.wait_ge(lat_ms, 1)
            lm = st[:, 4:8].rearrange("p (t g) -> p g t", g=2)
            step(nc.vector.tensor_scalar(lm[:, 0, :], lm[:, 0, :], 1.0 / QR, EPS, ALU.mult, ALU.add))
            nc.vector.tensor_scalar(lm[:, 1, :], lm[:, 1, :], 1.0 / KVR, EPS, ALU.mult, ALU.add).then_inc(lat_var, 1)
            dve.wait_ge(lat_std, 1)
            nc.vector.reciprocal(st[:, 4:8], st[:, 4:8]).then_inc(lat_rstd, 1)
            dve.wait_ge(trig_ready, 1)

            def rope(x1, x2, o1, o2, cs, sn, r1, r2):
                v.add(nc.vector.tensor_tensor(r1, x1, cs, ALU.mult))
                step(nc.vector.tensor_tensor(r2, x2, sn, ALU.mult))
                step(nc.vector.tensor_tensor(o1, r1, r2, ALU.subtract))
                v.add(nc.vector.tensor_tensor(r1, x2, cs, ALU.mult))
                step(nc.vector.tensor_tensor(r2, x1, sn, ALU.mult))
                return nc.vector.tensor_tensor(o2, r1, r2, ALU.add)

            k0 = QR + KVR
            for t in range(TT):
                cs, sn = cos[:, HALF * t:HALF * t + HALF], sin[:, HALF * t:HALF * t + HALF]
                step(rope(lat[:, t, k0:k0 + HALF], lat[:, t, k0 + HALF:k0 + ROPE],
                          kpad[:, 0, t, 0:HALF], kpad[:, 0, t, HALF:ROPE], cs, sn, rt[:, 0, 0:HALF], rt[:, 1, 0:HALF]))
            nc.vector.tensor_copy(kpad[:, 1, :, ROPE:P], kpad[:, 0, :, 0:ROPE]).then_inc(kpad_ready, 1)
            for k in range(10, 16):
                ada_sum(k)
            for t in range(TT):
                bank = full(dve, f"qpe{t}").rearrange("p (h n) -> p h n", h=H)
                q = qpe[:, t, :].rearrange("p (h n) -> p h n", h=H)
                cs = cos[:, HALF * t:HALF * t + HALF].unsqueeze(1).broadcast_to([P, H, HALF])
                sn = sin[:, HALF * t:HALF * t + HALF].unsqueeze(1).broadcast_to([P, H, HALF])
                r1, r2 = (rt[:, k, :].rearrange("p (h n) -> p h n", h=H) for k in range(2))
                v.add(nc.vector.tensor_tensor(r1, bank[:, :, 0:HALF], cs, ALU.mult))
                step(nc.vector.tensor_tensor(r2, bank[:, :, HALF:ROPE], sn, ALU.mult))
                step(nc.vector.tensor_tensor(q[:, :, 0:HALF], r1, r2, ALU.subtract))
                v.add(nc.vector.tensor_tensor(r1, bank[:, :, HALF:ROPE], cs, ALU.mult))
                ins = nc.vector.tensor_tensor(r2, bank[:, :, 0:HALF], sn, ALU.mult)
                empty(ins, f"qpe{t}")
                copied(dve, f"qpe{t}")
                nc.vector.tensor_tensor(q[:, :, HALF:ROPE], r1, r2, ALU.add).then_inc(qpe_ready, 1)
                dve.wait_ge(qpe_ready, t + 1)
            ada_finish(2, 2)

    JOBS = 2 * H
    neg_abs, log_term, decay_ready, log_weight, weight_exp, weights_ready = map(
        nc_sem, ("neg_abs", "log_term", "decay_ready", "log_weight", "weight_exp", "weights_ready"))
    row_max, row_exp, probs_ready, squares_ready, squares_summed, x2_loaded = map(
        nc_sem, ("row_max", "row_exp", "probs_ready", "squares_ready", "squares_summed", "x2_loaded"))
    SCALED, DECAY, WEIGHT = 0, 1, 2
    PROB, PROBT = 0, 1

    def diagonals(ap):
        return ap.rearrange("p (b n) -> p b n", n=P)[:, 0:3:2, :]

    def steps(k, *stages):
        return [(s, k - lag) for lag, s in stages if 0 <= k - lag < JOBS]

    with nc.Block() as block:
        @block.sync
        def _(sp):
            for n in range(2):
                load_group(sp, f"w_o{n}", wo_view, 512 * n, 512, KC)
            full(sp, "z14")
            sp.dma_start(x2[:, :, :], x_view).then_inc(x2_loaded, 16)

        @block.gpsimd
        def _(pool):
            ada_load_parts(pool, 16)

        @block.tensor
        def _(pe):
            def scores(j):
                h, bank = j // 2, take(pe, f"z{j}")
                if j % 2 == 0:
                    nc.tensor.matmul(bank[:, 0:T], sbk[:, h, 0:P], sbq[:, h, :], start=True, stop=True)
                    ins = nc.tensor.matmul(bank[:, T:T + P], sbk[:, h, P:T], sbq[:, h, P:T], start=True, stop=True)
                else:
                    for i in range(TT):
                        o = bank[:, P * i:P * i + P * (i + 1)]
                        nc.tensor.matmul(o, qnT[:, h, P * i:P * i + P], knT[:, h, 0:P * (i + 1)], start=True, stop=False)
                        ins = nc.tensor.matmul(o, qpeT[:, h // 2, P * i:P * i + P], kpeT[:, h % 2, 0:P * (i + 1)],
                                               start=False, stop=True)
                fill(ins, f"z{j}")

            def middle(j):
                k, bank = (j // 2) % 2, take(pe, f"r{j}")
                if j % 2 == 0:
                    pe.wait_ge(decay_ready, j // 2 + 1)
                    d = za[k][:, DECAY, :]
                    nc.tensor.matmul(bank[:, 0:T], tri[:, :], d[:, 0:T], start=True, stop=False)
                    nc.tensor.matmul(bank[:, P:T], ones[:, :], d[:, T:T + P], start=False, stop=True)
                    ins = nc.tensor.matmul(bank[:, T:T + P], tri[:, :], d[:, T:T + P], start=True, stop=True)
                else:
                    pe.wait_ge(probs_ready, j // 2 + 1)
                    for b in range(3):
                        ins = nc.tensor.transpose(bank[:, P * b:P * b + P], ma[k][:, PROB, P * b:P * b + P], ident[:, :])
                fill(ins, f"r{j}")

            def values(j):
                h, k = j // 2, (j // 2) % 2
                if j % 2 == 0:
                    pe.wait_ge(weights_ready, h + 1)
                    w, val = za[k][:, WEIGHT, :], sbv
                else:
                    copied(pe, f"r{j}")
                    w, val = ma[k][:, PROBT, :], vm
                bank = take(pe, f"o{j}")
                nc.tensor.matmul(bank[:, 0:T], val[:, 0, P * h:P * h + P], w[:, 0:T], start=True, stop=False)
                fill(nc.tensor.matmul(bank[:, P:T], val[:, 1, P * h:P * h + P], w[:, T:T + P], start=False, stop=True),
                     f"o{j}")

            def squares(j):
                pe.wait_ge(squares_ready, j + 1)
                nc.tensor.matmul(ps[:, 6 - j % 2, 0:T], ones[:, :], sq[:, j % 2, :], start=(j < 2),
                                 stop=(j >= JOBS - 2)).then_inc(squares_summed, 1)

            for b in (5, 6):
                pe.wait_ge(emptied[b], used[b])
            for k in range(JOBS + 5):
                for stage, j in steps(k, (0, scores), (2, middle), (4, values), (5, squares)):
                    stage(j)

        @block.scalar
        def _(act):
            def scaled(j):
                if j % 2 == 0:
                    b = full(act, f"z{j}")
                    empty(nc.scalar.activation(za[(j // 2) % 2][:, SCALED, :], b[:, 0:384], ACT.Copy, scale=SB_SCALE), f"z{j}")

            def first(j):
                h, k = j // 2, (j // 2) % 2
                if j % 2 == 0:
                    w = za[k][:, WEIGHT, :]
                    act.wait_ge(neg_abs, h + 1)
                    act_steps.add(nc.scalar.activation(w, w, ACT.Exp))
                    act_steps.wait(act)
                    nc.scalar.activation(w, w, ACT.Ln, bias=1.0).then_inc(log_term, 1)
                else:
                    act.wait_ge(row_max, h + 1)
                    for i in range(TT):
                        s = ma[k][:, PROB, P * i:P * i + P * (i + 1)]
                        ins = nc.scalar.activation(s, s, ACT.Exp, bias=mxd[:, k, 2 + i:3 + i], scale=MLA_SCALE,
                                                   accum_out=mxd[:, k, 4 + i:5 + i])
                    ins.then_inc(row_exp, 1)

            def second(j):
                h, k = j // 2, (j // 2) % 2
                if j % 2 == 0:
                    w = za[k][:, WEIGHT, :]
                    act.wait_ge(log_weight, h + 1)
                    nc.scalar.activation(w, w, ACT.Exp).then_inc(weight_exp, 1)
                else:
                    b = full(act, f"r{j}")
                    empty(nc.scalar.copy(ma[k][:, PROBT, :], b[:, 0:384]), f"r{j}")

            def head_out(j):
                m = mix[:, j // 2 + H * (j % 2), :]
                b = full(act, f"o{j}")
                empty(nc.scalar.copy(m, b[:, 0:T]), f"o{j}")
                copied(act, f"o{j}")
                if j >= 2:
                    act.wait_ge(squares_summed, j - 1)
                nc.scalar.activation(sq[:, j % 2, :], m, ACT.Square).then_inc(squares_ready, 1)

            nc.scalar.preload_act_table_set("natural_log_exp_and_others")
            for k in range(JOBS + 5):
                for stage, j in steps(k, (0, scaled), (1, first), (3, second), (4, head_out)):
                    stage(j)

        @block.vector
        def _(dve):
            v = vec_steps

            def step(ins):
                v.add(ins)
                v.wait(dve)

            def begin(j):
                h, k = j // 2, (j // 2) % 2
                if j % 2 == 0:
                    copied(dve, f"z{j}")
                    if h >= 2:
                        full(dve, f"o{j - 4}")
                    z = za[k][:, SCALED, :]
                    nc.vector.scalar_tensor_tensor(out=za[k][:, WEIGHT, :], in0=z, scalar=-1.0, in1=z,
                                                   op0=ALU.mult, op1=ALU.min).then_inc(neg_abs, 1)
                else:
                    b = full(dve, f"z{j}")
                    if h >= 2:
                        full(dve, f"r{j - 4}")
                    s = ma[k][:, PROB, :]
                    empty(nc.vector.tensor_tensor(s, b[:, 0:384], mask_mla[:, :], ALU.add), f"z{j}")
                    copied(dve, f"z{j}")
                    for i in range(TT):
                        v.add(nc.vector.reduce_max(mxd[:, k, i:i + 1], s[:, P * i:P * i + P * (i + 1)], AX.X))
                    v.wait(dve)
                    nc.vector.tensor_scalar(mxd[:, k, 2:4], mxd[:, k, 0:2], -MLA_SCALE, None, ALU.mult).then_inc(row_max, 1)

            def decay(j):
                h, k = j // 2, (j // 2) % 2
                if j % 2 == 0:
                    d = za[k][:, DECAY, :]
                    dve.wait_ge(log_term, h + 1)
                    step(nc.vector.scalar_tensor_tensor(out=d, in0=za[k][:, SCALED, :], scalar=0.0,
                                                        in1=za[k][:, WEIGHT, :], op0=ALU.max, op1=ALU.add))
                    nc.vector.tensor_tensor(diagonals(d), diagonals(d), mask_sb[:, :].unsqueeze(1).broadcast_to([P, 2, P]),
                                            ALU.mult).then_inc(decay_ready, 1)

            def second(j):
                h, k = j // 2, (j // 2) % 2
                if j % 2 == 0:
                    w = za[k][:, WEIGHT, :]
                    b = full(dve, f"r{j}")
                    empty(nc.vector.scalar_tensor_tensor(out=w, in0=b[:, 0:384], scalar=-1.0, in1=za[k][:, SCALED, :],
                                                         op0=ALU.mult, op1=ALU.add), f"r{j}")
                    copied(dve, f"r{j}")
                    nc.vector.tensor_scalar(w, w, 0.0, None, ALU.min).then_inc(log_weight, 1)
                else:
                    dve.wait_ge(row_exp, h + 1)
                    step(nc.vector.reciprocal(mxd[:, k, 6:8], mxd[:, k, 4:6]))
                    for i in range(TT):
                        s = ma[k][:, PROB, P * i:P * i + P * (i + 1)]
                        ins = nc.vector.tensor_scalar(s, s, mxd[:, k, 6 + i:7 + i], None, ALU.mult)
                    ins.then_inc(probs_ready, 1)

            def masked(j):
                h, k = j // 2, (j // 2) % 2
                if j % 2 == 0:
                    w = za[k][:, WEIGHT, :]
                    dve.wait_ge(weight_exp, h + 1)
                    nc.vector.tensor_tensor(diagonals(w), diagonals(w), mask_sb[:, :].unsqueeze(1).broadcast_to([P, 2, P]),
                                            ALU.mult).then_inc(weights_ready, 1)

            for k in range(JOBS + 5):
                for stage, j in steps(k, (1, decay), (2, second), (3, masked), (0, begin)):
                    stage(j)

    grp_var, grp_std, mix_ready, x2_part, x2_squared, x2_var, x2_std, x2_rstd, xs2_act, xs2_vec = map(
        nc_sem, ("grp_var", "grp_std", "mix_ready", "x2_part", "x2_squared", "x2_var", "x2_std", "x2_rstd", "xs2_act", "xs2_vec"))
    x2_stored, h2_high, a2_ready, sh2_ready, keys_loaded = map(
        nc_sem, ("x2_stored", "h2_high", "a2_ready", "sh2_ready", "keys_loaded"))

    def quarter(t, a, r):
        return t[QP * a:QP * a + QP, :].rearrange("p (q r) -> p r q", r=4)[:, r, :]

    def quartered(rows, t):
        return rows[:, t, :].rearrange("p (b a i) -> p a b i", a=4, i=QP)

    def in_quarters(rows, t):
        return rows[:, t, :].rearrange("p (a b i) -> p a b i", a=4, i=QP)

    def h2_evict(eng, u):
        bank = full(eng, f"h2T{u}")
        for k in range(2):
            ch = 2 * u + k
            if eng is nc.scalar:
                ins = nc.scalar.activation(h2T[:, ch, :], bank[:, T * k:T * k + T], ACT.Identity,
                                           bias=sh2q[:, ch:ch + 1], scale=a2q[:, ch:ch + 1])
            else:
                ins = nc.vector.tensor_scalar(h2T[:, ch, :], bank[:, T * k:T * k + T], a2q[:, ch:ch + 1],
                                              sh2q[:, ch:ch + 1], ALU.mult, ALU.add)
        empty(ins, f"h2T{u}")

    with nc.Block() as block:
        @block.sync
        def _(sp):
            load_group(sp, "w_o2", wo_view, 512 * 2, 512, KC)
            for s, k in enumerate((peer_keys1, peer_keys2)):
                sp.dma_start(knat[:, s, :, :], k[0].rearrange("h n q -> n h q")).then_inc(keys_loaded, 16)
            load_group(sp, "w_o3", wo_view, 512 * 3, 512, KC)
            load_wpq(sp, 0)
            sp.wait_ge(x2_part, 8)
            sp.dma_start(x2_dram, x2[:, :, :].rearrange("p t d -> p (t d)")).then_inc(x2_stored, 16)

        @block.gpsimd
        def _(pool):
            for a in range(4):
                for r in range(4):
                    ins = nc.gpsimd.tensor_copy(quarter(sh2q, a, r), modc[QP * r:QP * r + QP, SH2 + 4 * a:SH2 + 4 * a + 4])
            ins.then_inc(sh2_ready, 1)
            for k in range(17, 20):
                ada_load_parts(pool, k)

        @block.tensor
        def _(pe):
            for g in range(4):
                bank = take(pe, f"gb{g}")
                for q in range(4):
                    col = modc[:, G1 + 4 * g + q:G1 + 4 * g + q + 1]
                    ins = nc.tensor.matmul(bank[:, P * q:P * q + P], col.broadcast_to([P, P]), ident[:, :], start=True, stop=True)
                fill(ins, f"gb{g}")
            for n in range(4):
                w = group(pe, f"w_o{n}", 512, KC)
                for t in range(TT):
                    bank = take(pe, f"w{n}_{t}")
                    for k in range(KC):
                        if n + t == 0:
                            pe.wait_ge(mix_ready, k + 1)
                        ins = nc.tensor.matmul(bank, mix[:, k, P * t:P * t + P], w[:, k, :], start=(k == 0), stop=(k == KC - 1))
                    fill(ins, f"w{n}_{t}")
                ada_cols(16 + n, acc4)
            pe.wait_ge(xs2_act, 1)
            pe.wait_ge(xs2_vec, 1)
            for u in range(8):
                bank = take(pe, f"h2T{u}")
                for k in range(2):
                    for t in range(TT):
                        ins = nc.tensor.transpose(bank[:, T * k + P * t:T * k + P * t + P],
                                                  xs2[:, t, P * (2 * u + k):P * (2 * u + k) + P], ident[:, :])
                fill(ins, f"h2T{u}")

        @block.scalar
        def _(act):
            for g in range(4):
                b = full(act, f"gb{g}")
                empty(nc.scalar.copy(g1b[:, 512 * g:512 * g + 512], b), f"gb{g}")
            act.wait_ge(grp_var, 2)
            nc.scalar.activation(rs_g[:, :, :], rs_g[:, :, :], ACT.Sqrt).then_inc(grp_std, 1)
            for m in range(8):
                n, t = m // 2, m % 2
                act.wait_ge(x2_part, m + 1)
                if m:
                    act.wait_ge(x2_squared, m)
                nc.scalar.activation(junk2[:, :], x2[:, t, 512 * n:512 * n + 512], ACT.Square,
                                     accum_out=st[:, 8 + 4 * t + n:9 + 4 * t + n]).then_inc(x2_squared, 1)
            act.wait_ge(x2_var, 1)
            nc.scalar.activation(st[:, 2:4], st[:, 2:4], ACT.Sqrt).then_inc(x2_std, 1)
            act.wait_ge(x2_rstd, 1)
            nc.scalar.activation(quartered(xs2, 0), in_quarters(x2, 0), ACT.Copy, scale=st[:, 2:3]).then_inc(xs2_act, 1)
            act.wait_ge(a2_ready, 1)
            act.wait_ge(sh2_ready, 1)
            for u in range(0, 8, 2):
                h2_evict(nc.scalar, u)

        @block.vector
        def _(dve):
            v = vec_steps

            def step(ins):
                v.add(ins)
                v.wait(dve)

            for g in range(2):
                nc.vector.tensor_scalar(rs_g[:, g, :], ps[:, 6 - g, 0:T], 1.0 / (H * P), EPS, ALU.mult, ALU.add).then_inc(grp_var, 1)
            dve.wait_ge(grp_std, 1)
            step(nc.vector.reciprocal(rs_g[:, :, :], rs_g[:, :, :]))
            for h in range(2 * H):
                nc.vector.scalar_tensor_tensor(out=mix[:, h, :], in0=mix[:, h, :], scalar=vcB[:, 22 + h:23 + h],
                                               in1=rs_g[:, h // H, :], op0=ALU.mult, op1=ALU.mult).then_inc(mix_ready, 1)
            dve.wait_ge(x2_loaded, 16)
            copied(dve, "gb3")
            for m in range(8):
                n, t = m // 2, m % 2
                cols = slice(512 * n, 512 * n + 512)
                b = full(dve, f"w{n}_{t}")
                if m >= 2:
                    dve.wait_ge(x2_part, m - 1)
                empty(nc.vector.tensor_tensor(tmpo[:, m % 2, :], b, g1b[:, cols], ALU.mult), f"w{n}_{t}")
                copied(dve, f"w{n}_{t}")
                nc.vector.tensor_tensor(x2[:, t, cols], x2[:, t, cols], tmpo[:, m % 2, :], ALU.add).then_inc(x2_part, 1)
                if t == 0:
                    ada_sum(16 + n, acc4)
            dve.wait_ge(x2_squared, 8)
            step(nc.vector.reduce_sum(st[:, 0:2], st[:, 8:16].rearrange("p (t n) -> p t n", n=4), AX.X))
            nc.vector.tensor_scalar(st[:, 2:4], st[:, 0:2], 1.0 / D, EPS, ALU.mult, ALU.add).then_inc(x2_var, 1)
            dve.wait_ge(x2_std, 1)
            nc.vector.reciprocal(st[:, 2:4], st[:, 2:4]).then_inc(x2_rstd, 1)
            ada_finish(4, 1)
            dve.wait_ge(ada_bias, 3)
            for a in range(4):
                for r in range(4):
                    o, i, cols = quarter(a2q, a, r), slice(QP * r, QP * r + QP), slice(4 * a, 4 * a + 4)
                    ins = nc.vector.scalar_tensor_tensor(out=o, in0=modc[i, SC2:SC2 + KC][:, cols], scalar=1.0,
                                                         in1=vcA[i, KC:2 * KC][:, cols], op0=ALU.add, op1=ALU.mult)
            ins.then_inc(a2_ready, 1)
            dve.wait_ge(x2_rstd, 1)
            nc.vector.tensor_scalar(quartered(xs2, 1), in_quarters(x2, 1), st[:, 3:4], None, ALU.mult).then_inc(xs2_vec, 1)

            dve.wait_ge(a2_ready, 1)
            dve.wait_ge(sh2_ready, 1)
            for u in range(0, 8, 2):
                h2_evict(nc.vector, u + 1)

    g2_stored = nc_sem("g2_stored")
    u_loaded = [nc_sem(f"u{s}_loaded") for s in range(3)]
    v_loaded = [nc_sem(f"v{s}_loaded") for s in range(3)]
    u_view = peer_u[0].rearrange("(s q j) (a c) -> j a q s c", j=NTILES, q=QP, a=4)
    UP = 64

    def load_u_tile(eng, slot, tile):
        for a in range(4):
            eng.dma_start(ubuf[slot][QP * a:QP * a + QP, :].rearrange("q (s c) -> q s c", s=4), tile(a)).then_inc(u_loaded[slot], 16)

    v_view = peer_v[0].rearrange("(p j) d -> j p d", j=NTILES)

    with nc.Block() as block:
        @block.sync
        def _(sp):
            for n in range(1, 4):
                load_wpq(sp, n)
            load_u_tile(sp, 0, lambda a: u_view[0, a])
            load_u_tile(sp, 1, lambda a: u_view[1, a])
            sp.wait_ge(ada_columns, 24)
            load_u_tile(sp, 2, lambda a: u_view[2, a])
            copied(sp, "g2r")
            sp.dma_start(g2_dram.rearrange("o (r q) -> (o r) q", q=P), g2row[:, :]).then_inc(g2_stored, 16)
            sp.wait_ge(x2_stored, 16)

        @block.gpsimd
        def _(pool):
            for k in range(20, 24):
                ada_load_parts(pool, k)

        @block.tensor
        def _(pe):
            pe.wait_ge(keys_loaded, 32)
            for u in range(4):
                bank = take(pe, f"kT{u}")
                for q in range(4):
                    ins = nc.tensor.transpose(bank[:, P * q:P * q + P], knat[:, u // 2, 4 * (u % 2) + q, :], ident[:, :])
                fill(ins, f"kT{u}")

            def query(u):
                w = group(pe, f"w_pq{u // 2}", 512, KC)
                bank = take(pe, f"p{u}")
                for s in range(2):
                    b = 2 * (u % 2) + s
                    ins = contract(pe, "", bank[:, T * s:T * s + T], lambda k: w[:, k, P * b:P * b + P],
                                   lambda k: h2T[:, k, :], KC)
                fill(ins, f"p{u}")

            def score(u):
                copied(pe, f"p{u}")
                bank = take(pe, f"sc{u}")
                for s in range(2):
                    for t in range(TT):
                        ins = nc.tensor.matmul(bank[:, P * (2 * s + t):P * (2 * s + t) + P], pq[:, u % 2, s, P * t:P * t + P],
                                               kT[:, H * s + u, :], start=True, stop=True)
                fill(ins, f"sc{u}")

            query(0)
            for u in range(4):
                copied(pe, f"kT{u}")
            for u in range(H):
                if u + 1 < H:
                    query(u + 1)
                score(u)
                if u % 2:
                    ada_cols(20 + u // 2)
            pe.wait_ge(ada_bias, 4)
            fill(nc.tensor.transpose(take(pe, "g2r")[0:KC, 0:P], modc[:, G2:G2 + KC], ident[:, :]), "g2r")

        @block.scalar
        def _(act):
            for u in range(4):
                b = full(act, f"kT{u}")
                empty(nc.scalar.copy(kT[:, 4 * u:4 * u + 4, :].rearrange("p h n -> p (h n)"), b), f"kT{u}")

            def query(u):
                b = full(act, f"p{u}")
                if u >= 2:
                    full(act, f"sc{u - 2}")
                empty(nc.scalar.copy(pq[:, u % 2, :, :].rearrange("p s t -> p (s t)"), b), f"p{u}")

            query(0)
            for u in range(8):
                nc.scalar.copy(h2s[:, 2 * u:2 * u + 2, 0, :], h2T[:, 2 * u:2 * u + 2, :]).then_inc(h2_high, 1)
            act.wait_ge(x2_stored, 16)
            for u in range(H):
                if u + 1 < H:
                    query(u + 1)
                b = full(act, f"sc{u}")
                empty(nc.scalar.copy(s_all[:, :, 2 * u:2 * u + 2, :], b.rearrange("p (s t n) -> p t s n", s=2, t=TT)), f"sc{u}")

        @block.vector
        def _(dve):
            for k in range(20, 24):
                ada_sum(k)
                for u in range(2 * (k - 20), 2 * (k - 20) + 2):
                    dve.wait_ge(h2_high, u + 1)
                    c = slice(2 * u, 2 * u + 2)
                    vec_steps.add(nc.vector.tensor_tensor(h2s[:, c, 1, :], h2T[:, c, :], h2s[:, c, 0, :].bitcast(F32), ALU.subtract))
            ada_finish(5, 1)
            b = full(dve, "g2r")
            empty(nc.vector.tensor_copy(g2row[:, :], b[0:KC, 0:P]), "g2r")

    transposed, high_ready, multiplied, hid_ready = map(nc_sem, ("u_transposed", "u_high_ready", "u_multiplied", "hid_ready"))
    vec_low_ready, pool_low_ready = nc_sem("u_low_ready_by_vector"), nc_sem("u_low_ready_by_gpsimd")
    best_shifted, best_exp, gate_ready = map(nc_sem, ("best_shifted", "best_exp", "gate_ready"))
    FIRST, TURN, TOPK_TURNS, LAST = 2, 3, 2 * TT * H, 3
    TURNS = (NTILES - FIRST - LAST) // TURN
    assert FIRST + TURN * TURNS + LAST == NTILES
    POOL_LOW = (0, 1, 3)
    VEC_LOW = tuple(g for g in range(4) if g not in POOL_LOW)

    class Tile:

        def __init__(self, base, turn=0):
            self.base, self.turn = base, turn
            self.n = base + TURN * turn
            self.slot = base % 3

        def group(self, g):
            return 4 * self.n + g

        def early(self, n):
            return isinstance(self.n, int) and self.n < n

        def low_ready(self, g):
            sem, mine = (pool_low_ready, POOL_LOW) if g in POOL_LOW else (vec_low_ready, VEC_LOW)
            return sem, len(mine) * self.n + mine.index(g) + 1

    def low(eng, tile, g):
        eng.wait_ge(high_ready, tile.group(g) + 1)
        (nc.gpsimd if g in POOL_LOW else nc.vector).tensor_tensor(
            ulo[g][:, :], uT[g][:, :], uhi[g][:, :].bitcast(F32), ALU.subtract).then_inc(tile.low_ready(g)[0], 1)

    with nc.Block() as block:
        @block.sync
        def _(sp):
            def load_u(tile):
                sp.wait_ge(transposed, 4 * (tile.n - 2))
                load_u_tile(sp, tile.slot, lambda a: u_view[bass.ds(tile.n, 1), a].rearrange("o q s c -> (o q) s c"))

            sp.wait_ge(g2_stored, 16)
            with sp.Fori(0, TURNS) as i:
                for k in range(TURN):
                    load_u(Tile(3 + k, i))
            for j in range(3 + TURN * TURNS, NTILES):
                load_u(Tile(j))
            for j in range(3):
                sp.wait_ge(transposed, 4 * (NTILES - 3 + (j - NTILES) % 3 + 1))
                sp.dma_start(ubuf[j][:, :], v_view[j]).then_inc(v_loaded[j], 16)

        @block.tensor
        def _(pe):
            def multiply(tile, g):
                pe.wait_ge(*tile.low_ready(g))
                if g == 0 and not tile.early(3):
                    pe.wait_ge(hid_ready, tile.n - 2)
                bank = ps[:, 3 + tile.slot, 0:T]
                for q in range(4):
                    ch = 4 * g + q
                    for u, part in ((uhi, 0), (uhi, 1), (ulo, 0)):
                        ins = nc.tensor.matmul(bank, u[g][:, P * q:P * q + P], h2s[:, ch, part, :],
                                               start=(ch == 0 and u is uhi and part == 0), stop=(ch == KC - 1 and u is ulo))
                ins.then_inc(multiplied, 1)

            def body(tile):
                for g in range(4):
                    multiply(tile, g)

            for j in range(FIRST):
                body(Tile(j))
            with pe.Fori(0, TURNS) as i:
                for k in range(TURN):
                    body(Tile(FIRST + k, i))
            for j in range(NTILES - LAST, NTILES):
                body(Tile(j))

        @block.gpsimd
        def _(pool):
            def body(tile):
                for g in POOL_LOW:
                    low(pool, tile, g)

            for j in range(FIRST):
                body(Tile(j))
            with pool.Fori(0, TURNS) as i:
                for k in range(TURN):
                    body(Tile(FIRST + k, i))
            for j in range(NTILES - LAST, NTILES):
                body(Tile(j))

        @block.scalar
        def _(act):
            def high(tile, g):
                act.wait_ge(transposed, tile.group(g) + 1)
                nc.scalar.copy(uhi[g][:, :], uT[g][:, :]).then_inc(high_ready, 1)

            def gelu(tile):
                act.wait_ge(multiplied, 4 * tile.n + 4)
                nc.scalar.activation(hid[:, bass.ds(tile.n, 1), :].rearrange("p o t -> p (o t)"),
                                     ps[:, 3 + tile.slot, 0:T], ACT.Gelu).then_inc(hid_ready, 1)

            def body(tile, first=False):
                for g in range(4):
                    high(tile, g)
                    if not first and g == 2:
                        gelu(Tile(tile.base - 1, tile.turn))

            body(Tile(0), first=True)
            body(Tile(1))
            with act.Fori(0, TOPK_TURNS) as i:
                for k in range(TURN):
                    body(Tile(FIRST + k, i))
            act.wait_ge(best_shifted, 1)
            nc.scalar.activation(best[:, :, :], best[:, :, :], ACT.Exp).then_inc(best_exp, 1)
            nc.scalar.preload_act_table_set("gelu_and_others")
            act.wait_ge(gate_ready, 1)
            with act.Fori(0, TURNS - TOPK_TURNS) as i:
                for k in range(TURN):
                    body(Tile(FIRST + TURN * TOPK_TURNS + k, i))
            for j in range(NTILES - LAST, NTILES):
                body(Tile(j))
            gelu(Tile(NTILES - 1))

        @block.vector
        def _(dve):
            v = vec_steps

            def step(ins):
                v.add(ins)
                v.wait(dve)

            def transpose(tile, g):
                if g == 0:
                    dve.wait_ge(u_loaded[tile.slot], UP * (tile.base // 3 + 1 + tile.turn))
                if not tile.early(1):
                    dve.wait_ge(multiplied, tile.group(g) - 3)
                rows = ubuf[tile.slot][:, :].rearrange("p (s b i) -> p b s i", s=4, i=QP)[:, 4 * g:4 * g + 4]
                nc.vector.transpose(uT[g][:, :].rearrange("p (b s i) -> p b s i", b=4, s=4), rows).then_inc(transposed, 1)

            def fence():
                nc.vector.drain()

            def top16(part, side, src, again):
                first, second = ((tk_v[:, side, k:k + 8], tk_i[:, side, k:k + 8]) for k in (0, 8))
                if part == 0:
                    nc.vector.max(first[0], src)
                elif part == 1:
                    nc.vector.max_index(first[1], first[0], src)
                    nc.vector.match_replace(again, first[0], src, -3e38)
                elif part == 2:
                    nc.vector.max(second[0], again)
                else:
                    nc.vector.max_index(second[1], second[0], again)
                fence()

            s_rows = s_all[:, :, :, :].rearrange("p t b n -> p (t b n)")

            def topk_load(i):
                nc.vector.tensor_copy(wk[:, 0, :, :].rearrange("p s n -> p (s n)"), s_rows[:, bass.ds(i * 2 * NK, 2 * NK)])
                fence()

            def topk_candidates():
                nc.vector.tensor_tensor(cand[:, 0, :].rearrange("p (a b) -> p a b", b=TOPK),
                                        tk_v[:, 0, :].unsqueeze(2).broadcast_to([P, TOPK, TOPK]),
                                        tk_v[:, 1, :].unsqueeze(1).broadcast_to([P, TOPK, TOPK]), ALU.add)
                fence()

            def topk_places(i):
                nc.vector.tensor_scalar(tk_ab[:, 0, :], tk_i[:, 2, :], 4, None, ALU.logical_shift_right)
                nc.vector.tensor_scalar(tk_ab[:, 1, :], tk_i[:, 2, :], 15, None, ALU.bitwise_and)
                nc.vector.tensor_copy(best[:, bass.ds(i, 1), :].rearrange("p o k -> p (o k)"), tk_v[:, 2, :])
                fence()
                nc.vector.tensor_copy(tk_f[:, 0:2, :], tk_ab[:, :, :])
                nc.vector.tensor_copy(tk_f[:, 2:4, :], tk_i[:, 0:2, :])
                fence()

            def topk_match():
                nc.vector.tensor_tensor(oh[:, :, :], iota16[:, :].unsqueeze(1).broadcast_to([P, 2 * TOPK, TOPK]),
                                        tk_f[:, 0:2, :].rearrange("p s k -> p (s k)").unsqueeze(2).broadcast_to([P, 2 * TOPK, TOPK]),
                                        ALU.is_equal)
                fence()

            def topk_pick():
                m = oh[:, :, :].rearrange("p (s k) r -> p s k r", s=2)
                nc.vector.tensor_tensor(m, m, tk_f[:, 2:4, :].unsqueeze(2).broadcast_to([P, 2, TOPK, TOPK]), ALU.mult)
                fence()

            def topk_select(i):
                for s in range(2):
                    nc.vector.reduce_sum(sel[:, s, bass.ds(i, 1), :].rearrange("p o k -> p (o k)"),
                                         oh[:, TOPK * s:TOPK * s + TOPK, :], AX.X)
                fence()

            def topk(part, i):
                if part == 0:
                    topk_load(i)
                elif part < 9:
                    side = (part - 1) // 4
                    top16((part - 1) % 4, side, wk[:, 0, side, :], wk[:, 1, side, :])
                elif part == 9:
                    topk_candidates()
                elif part < 14:
                    top16(part - 10, 2, cand[:, 0, :], cand[:, 1, :])
                elif part == 15:
                    topk_places(i)
                elif part == 17:
                    topk_match()
                elif part == 19:
                    topk_pick()
                elif part == 21:
                    topk_select(i)

            def body(tile, turn=None, part=0, last=False):
                for g in range(4):
                    if g in VEC_LOW:
                        low(dve, tile, g)
                    if g < 2:
                        transpose(tile, g + 2)
                    elif not last:
                        transpose(Tile(tile.base + 1, tile.turn), g - 2)
                    if turn is not None:
                        topk(part + g, turn)

            transpose(Tile(0), 0)
            transpose(Tile(0), 1)
            body(Tile(0))
            body(Tile(1))
            with dve.Fori(0, TOPK_TURNS // 2) as i:
                for k in range(2 * TURN):
                    body(Tile(FIRST + k, 2 * i), turn=i, part=4 * k)
            step(nc.vector.tensor_copy(gsum[:, 0, :], best[:, :, 0]))
            nc.vector.tensor_tensor(best[:, :, :], best[:, :, :], gsum[:, 0, :].unsqueeze(2).broadcast_to([P, TT * H, TOPK]),
                                    ALU.subtract).then_inc(best_shifted, 1)
            dve.wait_ge(best_exp, 1)
            step(nc.vector.reduce_sum(gsum[:, 0, :], best[:, :, :], AX.X))
            step(nc.vector.reciprocal(gsum[:, 1, :], gsum[:, 0, :]))
            nc.vector.tensor_tensor(gate[:, :, :], best[:, :, :], gsum[:, 1, :].unsqueeze(2).broadcast_to([P, TT * H, TOPK]),
                                    ALU.mult).then_inc(gate_ready, 1)
            with dve.Fori(0, TURNS - TOPK_TURNS) as i:
                for k in range(TURN):
                    body(Tile(FIRST + TURN * TOPK_TURNS + k, i))
            for j in range(NTILES - LAST, NTILES):
                body(Tile(j), last=(j == NTILES - 1))

    slots_turned, slots_ready, columns_negated, distance_ready, slot_copied, slot_seen = map(
        nc_sem, ("slots_turned", "slots_ready", "columns_negated", "distance_ready", "slot_copied", "slot_seen"))
    rows_ready, columns_ready, fourth_ready, gates_made, gated = map(
        nc_sem, ("rows_ready", "columns_ready", "fourth_ready", "gates_made", "gated"))
    GT = 4
    MINE = GT - 1
    with nc.Block() as block:
        @block.tensor
        def _(pe):
            for b, src in ((0, sel[:, 0]), (1, sel[:, 1]), (2, gate)):
                for t in range(TT):
                    s = src[:, H * t:H * t + H, :].rearrange("p h k -> p (h k)")
                    ins = nc.tensor.transpose(ps[:, b, P * t:P * t + P], s, ident[:, :])
            ins.then_inc(slots_turned, 1)

            def gates(group, k, again):
                pe.wait_ge(rows_ready, group + 1)
                pe.wait_ge(columns_ready, group + 1)
                pe.wait_ge(fourth_ready, group + 1)
                if again:
                    pe.wait_ge(gated, group - 1)
                for q in range(GT):
                    ins = nc.tensor.matmul(ps[:, 3 + k, P * q:P * q + P], oneh1[:, k, q, :], oneh2[:, k, q, :],
                                           start=True, stop=True)
                ins.then_inc(gates_made, 1)

            for k in range(2):
                gates(k, k, False)
            with pe.Fori(0, T // (2 * GT) - 1) as i:
                for k in range(2):
                    gates(2 * i + 2 + k, k, True)

        @block.gpsimd
        def _(pool):
            pool.wait_ge(slots_ready, 3)

            def fourth(group, k, again):
                if again:
                    pool.wait_ge(gates_made, group - 1)
                nc.gpsimd.tensor_copy(slot[:, k, :].unsqueeze(2), selT[:, :, bass.ds(GT * group + MINE, 1)])\
                    .then_inc(slot_copied, 1)
                pool.wait_ge(slot_copied, group + 1)
                pool.sem_inc(slot_seen, 1)
                if k == 0:
                    nc.gpsimd.tensor_scalar(oneh1[:, k, MINE, :], iota[:, :], slot[:, k, 0:1], slot[:, k, 2:3],
                                            ALU.is_equal, ALU.mult)
                nc.gpsimd.tensor_scalar(oneh2[:, k, MINE, :], iota[:, :], slot[:, k, 1:2], None, ALU.is_equal)\
                    .then_inc(fourth_ready, 1)

            for k in range(2):
                fourth(k, k, False)
            with pool.Fori(0, T // (2 * GT) - 1) as i:
                for k in range(2):
                    fourth(2 * i + 2 + k, k, True)

        @block.scalar
        def _(act):
            act.wait_ge(slots_ready, 3)
            nc.scalar.activation(negT[:, :], selT[:, 1, :], ACT.Copy, scale=-1.0).then_inc(columns_negated, 1)
            act.wait_ge(columns_negated, 1)

            def columns(group, k, again):
                if again:
                    act.wait_ge(gates_made, group - 1)
                for q in range(MINE):
                    ins = nc.scalar.activation(oneh2[:, k, q, :], iota[:, :], ACT.Abs, bias=negT[:, bass.ds(GT * group + q, 1)])
                ins.then_inc(distance_ready, 1)
                act.wait_ge(distance_ready, group + 1)
                nc.scalar.activation(oneh2[:, k, 0:MINE, :], oneh2[:, k, 0:MINE, :], ACT.Relu, bias=1.0, scale=-1.0)\
                    .then_inc(columns_ready, 1)

            for k in range(2):
                columns(k, k, False)
            with act.Fori(0, T // (2 * GT) - 1) as i:
                for k in range(2):
                    columns(2 * i + 2 + k, k, True)

        @block.vector
        def _(dve):
            dve.wait_ge(slots_turned, 1)
            for b in range(3):
                nc.vector.tensor_copy(selT[:, b, :], ps[:, b, 0:T]).then_inc(slots_ready, 1)
            dve.wait_ge(slots_ready, 3)

            def rows(group, k):
                for q in range(MINE + k):
                    t = GT * group + q
                    ins = nc.vector.tensor_scalar(oneh1[:, k, q, :], iota[:, :], selT[:, 0, bass.ds(t, 1)],
                                                  selT[:, 2, bass.ds(t, 1)], ALU.is_equal, ALU.mult)
                ins.then_inc(rows_ready, 1)

            def gating(group, k):
                dve.wait_ge(gates_made, group + 1)
                h = hid[:, :, bass.ds(GT * group, GT)].rearrange("p j t -> p t j")
                nc.vector.tensor_tensor(h, h, ps[:, 3 + k, :].rearrange("p (t j) -> p t j", t=GT), ALU.mult).then_inc(gated, 1)

            for k in range(2):
                rows(k, k)
            with dve.Fori(0, T // (2 * GT) - 1) as i:
                for k in range(2):
                    gating(2 * i + k, k)
                    rows(2 * i + 2 + k, k)
            for k in range(2):
                gating(T // GT - 2 + k, k)

    v_high, v_low, h_high, h_low, down = map(nc_sem, ("v_high", "v_low", "hid_high", "hid_low", "down"))
    x2_back, g2_back, fg_loaded, y_scaled, y_added, y_squared, y_var, y_std, y_rstd, y_done, out_stored = map(
        nc_sem, ("x2_back", "g2_back", "fg_loaded", "y_scaled", "y_added", "y_squared", "y_var", "y_std", "y_rstd", "y_done", "out_stored"))
    VTURN, VFIRST = 6, 2

    class Down:

        def __init__(self, base, turn=0):
            self.base, self.turn, self.n = base, turn, base + VTURN * turn
            self.slot, self.buf, self.hbuf = base % 3, base % 2, base % 3

        def early(self, n):
            return isinstance(self.n, int) and self.n < n

    def down_tiles(eng, body):
        for j in range(VFIRST):
            body(Down(j))
        with eng.Fori(0, (NTILES - VFIRST) // VTURN) as i:
            for k in range(VTURN):
                body(Down(VFIRST + k, i))

    with nc.Block() as block:
        @block.sync
        def _(sp):
            def load_v(d):
                if not d.early(3):
                    sp.wait_ge(v_low, d.n - 2)
                    sp.dma_start(ubuf[d.slot][:, :], v_view[bass.ds(d.n, 1)].rearrange("o p d -> p (o d)"))\
                        .then_inc(v_loaded[d.slot], 16)

            for j in range(3, 8):
                load_v(Down(j))
            with sp.Fori(0, (NTILES - 8) // VTURN) as i:
                for k in range(VTURN):
                    load_v(Down(8 + k, i))
            sp.dma_start(x2r[:, :, :].rearrange("p t d -> p (t d)"), x2_dram).then_inc(x2_back, 16)
            sp.dma_start(g2b[:, :], g2_dram.broadcast_to([P, D])).then_inc(g2_back, 16)
            sp.dma_start(fgb[:, :], final_norm_g.rearrange("(o d) -> o d", o=1).broadcast_to([P, D])).then_inc(fg_loaded, 16)
            out_view = out[0].rearrange("(t p) d -> p t d", p=P)
            for t in range(TT):
                sp.wait_ge(y_done, t + 1)
                sp.dma_start(out_view[:, t, :], yo[:, t, :]).then_inc(out_stored, 16)
            sp.wait_ge(out_stored, 16 * TT)

        @block.tensor
        def _(pe):
            def body(d):
                pe.wait_ge(h_low, d.n + 1)
                pe.wait_ge(v_low, d.n + 1)
                for t in range(TT):
                    first = d.early(1)
                    for hpart, vpart in ((0, vhi), (0, vlo), (1, vhi)):
                        for c in range(4):
                            last = hpart == 1
                            ins = nc.tensor.matmul(ps[:, 4 * t + c, :], asp[:, d.hbuf, hpart, P * t:P * t + P],
                                                   vpart[:, d.buf, 512 * c:512 * c + 512],
                                                   start=(first and hpart == 0 and vpart is vhi), stop=last,
                                                   skip_group_check=True)
                ins.then_inc(down, 1)

            down_tiles(pe, body)

        @block.scalar
        def _(act):
            def body(d):
                act.wait_ge(v_loaded[d.slot], 16 * (d.base // 3 + 1 + 2 * d.turn))
                if not d.early(2):
                    act.wait_ge(down, d.n - 1)
                nc.scalar.copy(vhi[:, d.buf, :], ubuf[d.slot][:, :]).then_inc(v_high, 1)
                nc.scalar.copy(asp[:, d.hbuf, 0, :], hid[:, bass.ds(d.n, 1), :].rearrange("p o t -> p (o t)")).then_inc(h_high, 1)

            down_tiles(act, body)
            for m in range(8):
                t, c = m // 4, m % 4
                act.wait_ge(y_added, m + 1)
                if m:
                    act.wait_ge(y_squared, m)
                nc.scalar.activation(junk3[:, 0, :], yo[:, t, 512 * c:512 * c + 512], ACT.Square,
                                     accum_out=st[:, 8 + m:9 + m]).then_inc(y_squared, 1)
                if c == 3:
                    act.wait_ge(y_var, t + 1)
                    nc.scalar.activation(st[:, 2 + t:3 + t], st[:, 2 + t:3 + t], ACT.Sqrt).then_inc(y_std, 1)

        @block.vector
        def _(dve):
            v = vec_steps

            def step(ins):
                v.add(ins)
                v.wait(dve)

            def body(d):
                dve.wait_ge(h_high, d.n + 1)
                nc.vector.tensor_tensor(asp[:, d.hbuf, 1, :], hid[:, bass.ds(d.n, 1), :].rearrange("p o t -> p (o t)"),
                                        asp[:, d.hbuf, 0, :].bitcast(F32), ALU.subtract).then_inc(h_low, 1)
                dve.wait_ge(v_high, d.n + 1)
                nc.vector.tensor_tensor(vlo[:, d.buf, :], ubuf[d.slot][:, :], vhi[:, d.buf, :].bitcast(F32), ALU.subtract)\
                    .then_inc(v_low, 1)

            down_tiles(dve, body)
            dve.wait_ge(down, NTILES)
            dve.wait_ge(x2_back, 16)
            dve.wait_ge(g2_back, 16)
            dve.wait_ge(fg_loaded, 16)
            for t in range(TT):
                for c in range(4):
                    cols = slice(512 * c, 512 * c + 512)
                    nc.vector.tensor_tensor(yo[:, t, cols], ps[:, 4 * t + c, :], g2b[:, cols], ALU.mult).then_inc(y_scaled, 1)
                    dve.wait_ge(y_scaled, 4 * t + c + 1)
                    nc.vector.tensor_tensor(yo[:, t, cols], yo[:, t, cols], x2r[:, t, cols], ALU.add).then_inc(y_added, 1)
                dve.wait_ge(y_squared, 4 * t + 4)
                step(nc.vector.reduce_sum(st[:, t:t + 1], st[:, 8 + 4 * t:12 + 4 * t], AX.X))
                nc.vector.tensor_scalar(st[:, 2 + t:3 + t], st[:, t:t + 1], 1.0 / D, EPS, ALU.mult, ALU.add).then_inc(y_var, 1)
                dve.wait_ge(y_std, t + 1)
                nc.vector.reciprocal(st[:, 4 + t:5 + t], st[:, 2 + t:3 + t]).then_inc(y_rstd, 1)
                dve.wait_ge(y_rstd, t + 1)
                nc.vector.scalar_tensor_tensor(out=yo[:, t, :], in0=yo[:, t, :], scalar=st[:, 4 + t:5 + t], in1=fgb[:, :],
                                               op0=ALU.mult, op1=ALU.mult).then_inc(y_done, 1)
    ctx.close()


_INS = ["x", "c", "positions", "w_ada", "b_ada", "norm1_g", "w_in", "mla_q_norm_g", "w_uq", "mla_kv_norm_g", "w_ukv",
        "out_norm_sba_g", "out_norm_mla_g", "w_o", "norm2_g", "w_peer_q", "peer_keys1", "peer_keys2", "peer_u",
        "peer_v", "final_norm_g"]


def kernel(**inputs):
    import concourse.bacc as bacc
    from concourse.bass_utils import run_bass_kernel_spmd

    nc = bacc.Bacc("TRN2", target_bir_lowering=False, num_devices=1)
    arrays, args = {}, []
    for name in _INS:
        a = np.ascontiguousarray(inputs[name])
        arrays[f"in_{name}"] = a
        args.append(nc.dram_tensor(f"in_{name}", a.shape, mybir.dt.from_np(a.dtype), kind="ExternalInput").ap())
    args.append(nc.dram_tensor("out_0", (1, T, D), F32, kind="ExternalOutput").ap())
    build(nc, *args)
    r = run_bass_kernel_spmd(nc, [arrays], core_ids=[0])
    return r.results[0]["out_0"]
```
